# Optimizing a Trainium2 kernel written in Bass

```python
import math
import jax, jax.numpy as jnp
from jax import lax
import numpy as np

D_MODEL = 1024
BATCH = 1
SEQ = 128
DEPTH = 1
DEC_BATCH = 1
DEC_SEQ = 512
PAST_LEN = 128

GRID_W = 64
N_HEADS = 8
QK_DIM = 64
V_DIM = 2 * QK_DIM
QK_COLS = N_HEADS * 2 * QK_DIM
V_COLS = N_HEADS * V_DIM
AXIS_DIM = QK_DIM // 2
ROPE_BASE = 10000.0
CONV_W = D_MODEL
CONV_K = 3
N_GROUPS = 4
EXPERTS_PER_GROUP = 4
N_EXPERTS = N_GROUPS * EXPERTS_PER_GROUP
TOP_K = 2
D_EXPERT = 512
Q_BLOCK = 128
IN_COLS = 3 * CONV_W + 2 * QK_COLS + V_COLS + 2 * D_MODEL
EPS = 1e-6

kernel_name = "hybrid_diffusion_conv_diffattn_hmoe_step"

def rms_norm(x, g):
    xf = x.astype(jnp.float32)
    xf = xf * lax.rsqrt(jnp.mean(xf * xf, axis=-1, keepdims=True) + EPS)
    return xf.astype(x.dtype) * g

def short_conv3(u, w):
    up = jnp.pad(u, ((0, 0), (1, 1), (0, 0)))
    return w[0] * up[:, :-2] + w[1] * up[:, 1:-1] + w[2] * up[:, 2:]

def axial_rope(x):
    n_tok = x.shape[1]
    rows = n_tok // GRID_W
    pos_row = jnp.repeat(jnp.arange(rows, dtype=jnp.float32), GRID_W)
    pos_col = jnp.tile(jnp.arange(GRID_W, dtype=jnp.float32), rows)
    inv_freq = 1.0 / (ROPE_BASE ** (jnp.arange(0, AXIS_DIM, 2, dtype=jnp.float32) / AXIS_DIM))
    half = AXIS_DIM // 2

    def rot(xa, pos):
        ang = pos[:, None] * inv_freq[None, :]
        cos = jnp.cos(ang)[None, :, None, None, :].astype(xa.dtype)
        sin = jnp.sin(ang)[None, :, None, None, :].astype(xa.dtype)
        x1, x2 = xa[..., :half], xa[..., half:]
        return jnp.concatenate([x1 * cos - x2 * sin, x1 * sin + x2 * cos], axis=-1)

    return jnp.concatenate([rot(x[..., :AXIS_DIM], pos_row), rot(x[..., AXIS_DIM:], pos_col)], axis=-1)

def diff_attention(q, k, v, lam):
    b, lq = q.shape[0], q.shape[1]
    nblk = lq // Q_BLOCK
    scale = 1.0 / math.sqrt(QK_DIM)
    qb = q.reshape(b, nblk, Q_BLOCK, N_HEADS, 2, QK_DIM).transpose(1, 0, 2, 3, 4, 5)

    def one_block(qblk):
        s = jnp.einsum('bqhcd,bkhcd->bchqk', qblk, k).astype(jnp.float32) * scale
        p = jax.nn.softmax(s, axis=-1)
        a = p[:, 0] - lam * p[:, 1]
        return jnp.einsum('bhqk,bkhv->bqhv', a.astype(v.dtype), v)

    o = lax.map(one_block, qb)
    return o.transpose(1, 0, 2, 3, 4).reshape(b, lq, N_HEADS, V_DIM)

def hier_moe(h, w_grp, b_grp, w_exp, b_exp, w1, w3, w2):
    shp = h.shape
    t = h.reshape(-1, shp[-1])
    g_logit = (t @ w_grp + b_grp).astype(jnp.float32)
    g_prob = jax.nn.softmax(g_logit, axis=-1)
    _, g_idx = lax.top_k(g_logit, 1)
    g_p = jnp.take_along_axis(g_prob, g_idx, axis=-1)
    e_logit = (t @ w_exp + b_exp).astype(jnp.float32).reshape(-1, N_GROUPS, EXPERTS_PER_GROUP)
    e_sel = jnp.take_along_axis(e_logit, g_idx[:, :, None], axis=1)[:, 0]
    top_v, top_i = lax.top_k(e_sel, TOP_K)
    w_top = jax.nn.softmax(top_v, axis=-1) * g_p
    expert_id = g_idx * EXPERTS_PER_GROUP + top_i
    combine = jnp.sum(jax.nn.one_hot(expert_id, N_EXPERTS, dtype=jnp.float32) * w_top[..., None], axis=1)
    combine = combine.astype(t.dtype)
    y = jnp.zeros_like(t)
    for e in range(N_EXPERTS):
        he = jax.nn.silu(t @ w1[e]) * (t @ w3[e])
        y = y + combine[:, e:e + 1] * (he @ w2[e])
    return y.reshape(shp)

def layer_forward(x, mod, is_latent, ctx_k, ctx_v, lam, lam_init,
                  norm1_g, w_in, conv_w, w_conv_out, q_norm_g, k_norm_g, subln_g,
                  w_attn_out, w_o, norm2_g, w_grp, b_grp, w_exp, b_exp, w1, w3, w2):
    b, l = x.shape[0], x.shape[1]
    shift1, scale1, gate1, shift2, scale2, gate2 = jnp.split(mod, 6, axis=-1)
    h = rms_norm(x, norm1_g) * (1 + scale1) + shift1
    z = h @ w_in
    sizes = [CONV_W, CONV_W, CONV_W, QK_COLS, QK_COLS, V_COLS, D_MODEL]
    idx = list(np.cumsum(sizes))
    cb, cc, cx, q, k, v, gc, ga = jnp.split(z, idx, axis=-1)
    y_conv = (cb * short_conv3(cc * cx, conv_w)) @ w_conv_out
    q = rms_norm(q.reshape(b, l, N_HEADS, 2, QK_DIM), q_norm_g)
    k = rms_norm(k.reshape(b, l, N_HEADS, 2, QK_DIM), k_norm_g)
    v = v.reshape(b, l, N_HEADS, V_DIM)
    if is_latent:
        q = axial_rope(q)
        k_lat = axial_rope(k)
        k_all = jnp.concatenate([k_lat, ctx_k], axis=1)
        v_all = jnp.concatenate([v, ctx_v], axis=1)
    else:
        k_all, v_all = k, v
    o = diff_attention(q, k_all, v_all, lam)
    o = rms_norm(o, subln_g) * (1.0 - lam_init)
    y_attn = o.reshape(b, l, V_COLS) @ w_attn_out
    mixed = jax.nn.sigmoid(gc) * y_conv + jax.nn.sigmoid(ga) * y_attn
    x = x + gate1 * (mixed @ w_o)
    h2 = rms_norm(x, norm2_g) * (1 + scale2) + shift2
    x = x + gate2 * hier_moe(h2, w_grp, b_grp, w_exp, b_exp, w1, w3, w2)
    return x, k, v

def setup_inputs(seed: int = 0) -> dict:
    key = jax.random.key(seed)
    ks = jax.random.split(key, 32)
    f32 = jnp.float32

    def nrm(k, shape, scale=1.0):
        return jax.random.normal(k, shape, f32) * scale

    d = D_MODEL
    return {
        "x_prompt": nrm(ks[0], (BATCH, SEQ, d)),
        "x_sample": nrm(ks[1], (DEC_BATCH, DEC_SEQ, d)),
        "cache_k": nrm(ks[2], (DEC_BATCH, DEPTH, PAST_LEN, N_HEADS, 2, QK_DIM)),
        "cache_v": nrm(ks[3], (DEC_BATCH, DEPTH, PAST_LEN, N_HEADS, V_DIM)),
        "c": nrm(ks[4], (DEC_BATCH, d)),
        "c_ctx": nrm(ks[5], (d,)),
        "w_ada": nrm(ks[6], (DEPTH, d, 6 * d), d ** -0.5),
        "b_ada": nrm(ks[7], (DEPTH, 6 * d), 0.02),
        "norm1_g": 1.0 + nrm(ks[8], (DEPTH, d), 0.02),
        "w_in": nrm(ks[9], (DEPTH, d, IN_COLS), d ** -0.5),
        "conv_w": nrm(ks[10], (DEPTH, CONV_K, CONV_W), CONV_K ** -0.5),
        "w_conv_out": nrm(ks[11], (DEPTH, CONV_W, d), CONV_W ** -0.5),
        "q_norm_g": 1.0 + nrm(ks[12], (DEPTH, QK_DIM), 0.02),
        "k_norm_g": 1.0 + nrm(ks[13], (DEPTH, QK_DIM), 0.02),
        "lambda_q1": nrm(ks[14], (DEPTH, QK_DIM), 0.1),
        "lambda_k1": nrm(ks[15], (DEPTH, QK_DIM), 0.1),
        "lambda_q2": nrm(ks[16], (DEPTH, QK_DIM), 0.1),
        "lambda_k2": nrm(ks[17], (DEPTH, QK_DIM), 0.1),
        "subln_g": 1.0 + nrm(ks[18], (DEPTH, V_DIM), 0.02),
        "w_attn_out": nrm(ks[19], (DEPTH, V_COLS, d), V_COLS ** -0.5),
        "w_o": nrm(ks[20], (DEPTH, d, d), d ** -0.5),
        "norm2_g": 1.0 + nrm(ks[21], (DEPTH, d), 0.02),
        "w_grp": nrm(ks[22], (DEPTH, d, N_GROUPS), d ** -0.5),
        "b_grp": nrm(ks[23], (DEPTH, N_GROUPS), 0.01),
        "w_exp": nrm(ks[24], (DEPTH, d, N_EXPERTS), d ** -0.5),
        "b_exp": nrm(ks[25], (DEPTH, N_EXPERTS), 0.01),
        "w1": nrm(ks[26], (DEPTH, N_EXPERTS, d, D_EXPERT), d ** -0.5),
        "w3": nrm(ks[27], (DEPTH, N_EXPERTS, d, D_EXPERT), d ** -0.5),
        "w2": nrm(ks[28], (DEPTH, N_EXPERTS, D_EXPERT, d), D_EXPERT ** -0.5),
    }

def reference(x_prompt, x_sample, cache_k, cache_v, c, c_ctx,
              w_ada, b_ada, norm1_g, w_in, conv_w, w_conv_out, q_norm_g, k_norm_g,
              lambda_q1, lambda_k1, lambda_q2, lambda_k2, subln_g, w_attn_out, w_o,
              norm2_g, w_grp, b_grp, w_exp, b_exp, w1, w3, w2):
    xp = x_prompt
    xs = x_sample
    new_k_list = []
    new_v_list = []
    for l in range(DEPTH):
        lam_init = 0.8 - 0.6 * math.exp(-0.3 * l)
        lam = (jnp.exp(jnp.sum((lambda_q1[l] * lambda_k1[l]).astype(jnp.float32)))
               - jnp.exp(jnp.sum((lambda_q2[l] * lambda_k2[l]).astype(jnp.float32)))
               + lam_init)
        mod_ctx = (jax.nn.silu(c_ctx) @ w_ada[l] + b_ada[l])[None, None, :]
        mod_lat = (jax.nn.silu(c) @ w_ada[l] + b_ada[l])[:, None, :]
        shared = (norm1_g[l], w_in[l], conv_w[l], w_conv_out[l], q_norm_g[l], k_norm_g[l],
                  subln_g[l], w_attn_out[l], w_o[l], norm2_g[l], w_grp[l], b_grp[l],
                  w_exp[l], b_exp[l], w1[l], w3[l], w2[l])
        xp, k_ctx, v_ctx = layer_forward(xp, mod_ctx, False, None, None, lam, lam_init, *shared)
        new_k_list.append(k_ctx)
        new_v_list.append(v_ctx)
        xs, _, _ = layer_forward(xs, mod_lat, True, cache_k[:, l], cache_v[:, l], lam, lam_init, *shared)
    new_k = jnp.stack(new_k_list, axis=1)
    new_v = jnp.stack(new_v_list, axis=1)
    return (xp, xs, new_k, new_v)


_drawn_inputs = setup_inputs


def setup_inputs(seed=0):
    import zlib

    import numpy as np

    out = dict(_drawn_inputs(seed))
    spreads = {}
    factors = {'q_norm_g': 6.288,
     'k_norm_g': 2.826,
     'lambda_q1': 8.0,
     'lambda_q2': 4.457,
     'lambda_k2': 3.253,
     'subln_g': 13.319,
     'b_grp': 15.51,
     'b_exp': 14.283,
     'cache_k': 8.0,
     'cache_v': 8.0,
     'norm2_g': 3.943}
    for name, (base, spread) in spreads.items():
        noise = np.random.default_rng([zlib.crc32(name.encode()), seed]).standard_normal(out[name].shape)
        drawn = base * np.exp(spread * noise) if base else spread * noise
        out[name] = __import__('jax').numpy.asarray(drawn.astype(out[name].dtype))
    for name, factor in factors.items():
        out[name] = (out[name] * factor).astype(out[name].dtype)
    return out
```

```python
import math
from contextlib import ExitStack

import numpy as np
import concourse.bass as bass
from concourse import mybir

P = 128
D = 1024
N_LAT = 512
N_CTX = 128
T = N_LAT + N_CTX
NT = T // P
CTX = NT - 1
KT = D // P
HEADS = 8
QK = 64
GROUP_HEADS = 4
GROUPS = HEADS // GROUP_HEADS
GW = GROUP_HEADS * P
KEYS = T
KCOLS = KEYS + N_CTX
EXPERTS = 16
EGROUPS = 4
FF = 512
SLOTS = 128
CHUNKS = T // SLOTS
CH = 4096
PAIRS_ALL = 2 * T
W_SLOTS = 4
EPS = 1e-6
LAM_INIT = 0.8 - 0.6 * math.exp(0.0)
SM_SCALE = 1.0 / math.sqrt(QK)
BIG = 1e30

COL = {}
for _name, _n in (("b_ada", 48), ("g1", 8), ("g2", 8), ("conv", 24), ("subln", 1), ("cT", 16), ("tokid", NT)):
    COL[_name] = (sum(n for _, n in COL.values()), _n)
COLS = sum(n for _, n in COL.values())
ROW = {}
for _name, _n in (("qg", 64), ("kg", 64), ("lam", 256), ("b_route", 20), ("desc", 4), ("ebase", 16)):
    ROW[_name] = (sum(n for _, n in ROW.values()), _n)
ROWS = sum(n for _, n in ROW.values())


def weight_chunks():
    names = [("ada", n) for n in range(4)]
    for g in range(GROUPS):
        names += [("in", 6 + g), ("in", 8 + g), ("in", 10 + g)]
        names += [("ada", 4 + 4 * g + n) for n in range(4)]
    for c in range(2):
        names += [("in", 2 + c), ("in", 4 + c), ("in", c)]
    for c in range(2):
        names += [("in", 12 + c), ("conv", c), ("in", 14 + c), ("attn", c)]
    return names + [("o", 0), ("o", 1)]


def psum_jobs():
    def ada(lo):
        made = []
        for n in range(lo, lo + 4):
            made.append(("ada", n, "act"))
            if n > lo:
                made.append(("adaT", n - 1, "dve"))
        return made + [("adaT", lo + 3, "dve")]

    jobs = ada(0)
    jobs += [("xT", k, "dve" if k % 2 == 0 else "act") for k in range(KT)]
    for g in range(GROUPS):
        for z in range(2 * NT):
            jobs.append(("qk", 2 * NT * g + z, "dve"))
            if z:
                jobs.append(("qkT", 2 * NT * g + z - 1, "act"))
        jobs.append(("v", NT * g, "act"))
        jobs.append(("qkT", 2 * NT * g + 2 * NT - 1, "act"))
        jobs.append(("kcT", g, "act"))
        jobs += [("v", NT * g + i, "act") for i in range(1, NT)]
        jobs += ada(4 + 4 * g)
    jobs.append(("rowsT", 0, "act"))
    for n in range(KT):
        jobs += [("cc", n, "act"), ("cx", n, "dve"), ("cb", n, "dve")]
    jobs += [("oT", j, "act") for j in range(2 * NT)]
    for n in range(KT):
        jobs += [("gc", n, "act"), ("cv", n, "dve"), ("ga", n, "act"), ("at", n, "dve")]
    jobs += [("wo", j, "dve") for j in range(2 * NT)]
    jobs += [("h2T", i, "act") for i in range(NT)]
    return jobs + [("route", 0, "dve"), ("rank", 0, "dve")]


JOBS = psum_jobs()
INDEX = {(kind, n): j for j, (kind, n, _) in enumerate(JOBS)}
EMPTIED = []
_count = {"dve": 0, "act": 0}
for _, _, _who in JOBS:
    _count[_who] += 1
    EMPTIED.append((_who, _count[_who]))
CHUNK_LIST = weight_chunks()
CHUNK = {name: n for n, name in enumerate(CHUNK_LIST)}
PAIRS = 4
XG = 4


def last_use(name):
    kind, n = name
    if kind == "ada":
        return INDEX[name]
    if kind == "o":
        return INDEX[("wo", NT * n + NT - 1)]
    if kind in ("conv", "attn"):
        return INDEX[({"conv": "cv", "attn": "at"}[kind], 4 * n + 3)]
    what, part = divmod(n, 2)
    if what in (3, 4):
        return INDEX[("qk", 2 * NT * part + NT * (what - 3) + NT - 1)]
    if what == 5:
        return INDEX[("v", NT * part + NT - 1)]
    return INDEX[({0: "cb", 1: "cc", 2: "cx", 6: "gc", 7: "ga"}[what], 4 * part + 3)]


def build(nc, io):
    f32, i32, u32 = mybir.dt.float32, mybir.dt.int32, mybir.dt.uint32
    ALU, ACT, AX = mybir.AluOpType, mybir.ActivationFunctionType, mybir.AxisListType.X
    mult, add, sub = ALU.mult, ALU.add, ALU.subtract

    with ExitStack() as ctx:
        def sb(name, cols, dt=f32, rows=P):
            return ctx.enter_context(nc.sbuf_tensor(name, [rows, cols], dt))

        def sem(name):
            return ctx.enter_context(nc.semaphore(name))

        ring = sb("weight_ring", W_SLOTS * CH)
        x_sb = sb("x", NT * D)
        cols = sb("cols", COLS)
        rows = sb("rows", ROWS)
        mod = sb("mod", 96)
        rwts = sb("router_weights", KT * 20)
        ident = sb("ident", P)
        ones = sb("ones", P)
        tri = sb("tri", P)
        silu_c = sb("silu_c", 16)
        ada_rows = [sb(f"ada_rows{b}", 512, rows=2) for b in range(2)]
        a1 = sb("scale1_g", 16)
        rowpack = sb("rowpack", 64)
        rowpackT = sb("rowpackT", P, rows=64)
        stat = sb("stat", 3 * NT)
        ropeC = sb("ropeC", 2 * 4 * 64)
        ropeS = sb("ropeS", 2 * 4 * 64)
        eps = sb("eps", 1)
        neglam = sb("neglam", 8)
        qkstat = sb("qkstat", 2 * 16)
        sm = sb("softmax_stats", 2 * 8)
        ostat = sb("ostat", 2 * NT * HEADS)
        no_pair = sb("no_pair", 80, u32)
        idx = sb("slot_tokens", EXPERTS * CHUNKS, u32)
        idxp = sb("slot_pairs", EXPERTS * CHUNKS, u32)
        idxc = sb("slot_now", 2, u32)
        unused = sb("unused", 1)
        comb = sb("pair_weights", 2 * NT)
        pos = sb("pair_table_rows", 2 * NT, u32)
        pair_ids = sb("pair_ids", 2 * NT, u32)
        meta = sb("expert_counts", 48, i32)

        arena = sb("arena", 10240 + 17408)
        Z = 10240

        def at(off, n, rows_=P):
            return arena[0:rows_, off:off + n]

        hT = at(0, KT * T).rearrange("p (k t) -> p k t", k=KT)
        o_tok = at(5120, NT * D).rearrange("p (i n) -> p i n", i=NT)
        qT = at(Z, 2560).rearrange("p (h t) -> p h t", h=GROUP_HEADS)
        kT = at(Z + 2560, 3072).rearrange("p (h t) -> p h t", h=GROUP_HEADS)
        v_sb = at(Z + 5632, 3072).rearrange("p (i n) -> p i n", i=NT + 1)
        prob = [at(Z + 8704 + 1280 * b, 1280).rearrange("p (c k) -> p c k", c=2) for b in range(2)]
        amix = [at(Z + 11264 + 640 * b, 640) for b in range(2)]
        aT = [at(Z + 12544 + 640 * b, 640) for b in range(2)]
        qk_n = [at(Z + 13824 + 512 * b, 512) for b in range(2)]
        qk_s = [at(Z + 14848 + 512 * b, 512) for b in range(2)]
        qk_r = [at(Z + 15872 + 512 * b, 512) for b in range(2)]
        kc = at(Z + 16896, 512)
        ropet = at(Z + 8704, 512)
        xn = at(5120, NT * D).rearrange("p (i n) -> p i n", i=NT)
        oT = at(Z, KT * T).rearrange("p (k t) -> p k t", k=KT)
        uT = at(Z + 5120, KT * T).rearrange("p (k t) -> p k t", k=KT)
        mixT = at(5120, KT * T).rearrange("p (k t) -> p k t", k=KT)
        PADW = T + 4
        t_cc = [at(Z + 10240 + 640 * b, 640) for b in range(2)]
        t_m = [at(Z + 11520 + PADW * b, PADW) for b in range(2)]
        t_cv = [at(Z + 12808 + 642 * b, 642) for b in range(2)]
        gate1 = at(Z + 10240, 2048).rearrange("p (v n) -> p v n", v=2)
        t_gc = at(Z + 14336, 640)
        t_ga = at(Z + 14976, 640)
        t_at = at(Z + 15616, 640)
        t_wo = at(Z + 16256, 512)
        mod2 = at(0, 4096).rearrange("p (s v n) -> p s v n", s=2, v=2)
        h2 = at(Z + 5120, NT * D).rearrange("p (i n) -> p i n", i=NT)
        h2T = at(Z, KT * T).rearrange("p (i k t) -> p i k t", i=NT, k=KT)
        down = [at(5120, CH), at(Z + 10240, CH)]
        rt = at(Z + 14336, 3072)
        xg = [at(1024 * b, 1024) for b in range(XG)]
        xgT = at(4096, 1024).rearrange("p (k s) -> p k s", k=KT)
        sg = at(Z, 512)
        hh = at(Z + 512, 512)
        hhT = at(Z + 1024, 512).rearrange("p (k s) -> p k s", k=4)
        ys = [at(Z + 1536 + 1024 * b, 1024) for b in range(2)]
        gate2 = at(Z + 5120, 2048).rearrange("p (v n) -> p v n", v=2)
        slot = [ring[:, CH * s:CH * (s + 1)] for s in range(W_SLOTS)]
        yg = [ring[:, 1024 * j:1024 * (j + 1)] for j in range(2 * NT)]

        psum = ctx.enter_context(nc.psum_tensor("psum", [P, 4096], f32))
        pair = [psum[:, 1024 * j:1024 * (j + 1)] for j in range(PAIRS)]

        def col(name):
            return cols[:, COL[name][0]:COL[name][0] + COL[name][1]]

        def row(name):
            return rows[:, ROW[name][0]:ROW[name][0] + ROW[name][1]]

        rows_dram, h2_dram, y_dram, table_dram = io["rows_scratch"], io["h2_scratch"], io["y_scratch"], io["table_scratch"]
        table_rows = table_dram.rearrange("s e -> (s e)").unsqueeze(1)

        def chunk_src(name):
            kind, n = name
            w = {"ada": io["w_ada"], "in": io["w_in"], "conv": io["w_conv_out"], "attn": io["w_attn_out"], "o": io["w_o"]}[kind]
            return w[:, 512 * n:512 * (n + 1)].rearrange("(k p) n -> p k n", p=P)

        def up_src(w, e):
            return w[e].rearrange("(k p) n -> p k n", p=P)

        def down_src(e):
            return io["w2"][e].rearrange("(k p) n -> p k n", p=P)

        s_cols, s_rows, s_rope, s_rwts = sem("cols_loaded"), sem("rows_loaded"), sem("rope_loaded"), sem("router_loaded")
        s_x = sem("x_loaded")
        s_kc = [sem(f"cached_k_loaded{g}") for g in range(GROUPS)]
        s_vc = [sem(f"cached_v_loaded{g}") for g in range(GROUPS)]
        s_w = [sem(f"weights_loaded{s}") for s in range(W_SLOTS)]
        s_job = sem("psum_job_done")
        s_emptied = {"dve": sem("emptied_by_dve"), "act": sem("emptied_by_act")}
        s_pool, s_dve, s_act = sem("pool_steps"), sem("dve_steps"), sem("act_steps")
        s_const = sem("constants_made")
        s_silu, s_siluc = sem("silu_act"), sem("silu_c_made")
        s_mod1 = sem("mod1_ready")
        s_xss, s_xsd, s_xrs, s_xn = sem("x_squares"), sem("x_sqrt"), sem("x_rstd"), sem("xn_ready")
        s_lamx, s_lame = sem("lam_sums"), sem("lam_exp")
        s_ropek = sem("rope_tables")
        s_sq, s_ss, s_sd, s_zn, s_m1, s_zr = (sem(n) for n in ("qk_squares", "qk_sums", "qk_sqrt", "qk_normed", "qk_cos_part", "qk_roped"))
        s_nk, s_nv = sem("new_k_stored"), sem("new_v_stored")
        s_half = sem("first_half_scores")
        s_scores, s_max, s_exp, s_mix = sem("scores"), sem("maxes"), sem("exps"), sem("mixed_probs")
        s_aTp, s_aT, s_pv, s_o = sem("probs_transposed"), sem("probsT_copied"), sem("pv_done"), sem("o_copied")
        s_oss, s_osd, s_on = sem("o_squares"), sem("o_sqrt"), sem("o_normed")
        s_rowpack, s_rowsT, s_rowsout = sem("rowpack_ready"), sem("rowsT_copied"), sem("rows_stored")
        s_g1rows, s_m2rows, s_g2rows = sem("gate1_rows"), sem("mod2_rows"), sem("gate2_rows")
        s_uT, s_ccp = sem("conv_ready"), sem("cc_ready")
        s_gc, s_ga, s_mixT = sem("gate_conv"), sem("gate_attn"), sem("merged")
        s_x2 = sem("x2_ready")
        s_x2ss, s_x2sd, s_h2m, s_h2, s_h2out = sem("x2_squares"), sem("x2_sqrt"), sem("h2_scaled"), sem("h2_ready"), sem("h2_stored")
        s_rexp_in, s_rexp, s_mask, s_pos = sem("route_exp_in"), sem("route_exp"), sem("masks_ready"), sem("pos_ready")
        s_zero, s_tabz, s_tab, s_idx, s_meta = sem("zeros_made"), sem("table_zeroed"), sem("table_scattered"), sem("table_loaded"), sem("meta_ready")
        s_slot = sem("slot_tokens_ready")
        s_xg = [sem(f"tokens_gathered{b}") for b in range(XG)]
        s_T, s_xgT, s_gu, s_sg, s_hh, s_HT, s_hhT, s_d = (sem(n) for n in (
            "xg_transposed", "xgT_copied", "gate_up_done", "silu_done", "hidden_ready", "hidden_transposed", "hiddenT_copied", "down_done"))
        s_ydve, s_yact = sem("y_left_copied"), sem("y_right_copied")
        s_wgu = [sem(f"gate_up_loaded{b}") for b in range(2)]
        s_wd = [sem(f"down_loaded{b}") for b in range(2)]
        s_yst = [sem(f"y_stored{b}") for b in range(2)]
        s_ofx, s_ofw, s_ofy, s_ofst = sem("more_tokens_gathered"), sem("more_weights_loaded"), sem("more_y_stored"), sem("more_y_confirmed")
        s_yg = [sem(f"y_gathered{i}") for i in range(NT)]
        s_out, s_outx = sem("out_ready"), sem("out_stored")

        block = ctx.enter_context(nc.Block())

        def emptied(eng, j):
            who, count = EMPTIED[j]
            eng.wait_ge(s_emptied[who], count)

        def job_done(eng, kind, n):
            eng.wait_ge(s_job, INDEX[(kind, n)] + 1)

        def job_psum(kind, n):
            return pair[INDEX[(kind, n)] % PAIRS]

        def more_chunks(eng, body):
            eng.wait_ge(s_meta, 1)
            total = eng.value_load(meta[0:1, 32:33], min_val=0, max_val=EXPERTS * CHUNKS)
            with eng.If(total > 0):
                with eng.Fori(0, EXPERTS) as e:
                    count = eng.value_load(meta[0:1, bass.ds(e, 1)], min_val=0, max_val=T)
                    base = eng.value_load(meta[0:1, bass.ds(e + 16, 1)], min_val=0, max_val=EXPERTS * CHUNKS)
                    with eng.Fori(1, CHUNKS) as c:
                        with eng.If(count > c * SLOTS):
                            body(e, c, base + c - 1)

        @block.sync
        def _(sp):
            sp.dma_start(cols[:, :], io["cols"]).then_inc(s_cols, 16)
            sp.dma_start(rows[:, :], io["rows"].to_broadcast([P, ROWS])).then_inc(s_rows, 16)

            def load_chunk(n):
                if n >= W_SLOTS:
                    sp.wait_ge(s_job, last_use(CHUNK_LIST[n - W_SLOTS]) + 1)
                sp.dma_start(slot[n % W_SLOTS].rearrange("p (k n) -> p k n", k=KT), chunk_src(CHUNK_LIST[n])).then_inc(s_w[n % W_SLOTS], 16)

            load_chunk(0)
            sp.dma_start(x_sb[:, 0:4 * D].rearrange("p (i n) -> p i n", i=4), io["x_sample"].rearrange("(i p) n -> p i n", p=P)).then_inc(s_x, 16)
            sp.dma_start(x_sb[:, 4 * D:], io["x_prompt"]).then_inc(s_x, 16)
            for n in range(1, 4):
                load_chunk(n)
            sp.dma_start(ropet, io["rope"]).then_inc(s_rope, 16)
            sp.dma_start(rwts[:, :], io["w_route"]).then_inc(s_rwts, 16)

            for n in range(4, 24):
                load_chunk(n)
            sp.wait_ge(s_rowsT, 1)
            sp.dma_start(rows_dram, rowpackT[:, :]).then_inc(s_rowsout, 16)
            sp.wait_ge(s_rowsout, 16)
            for n in range(24, 30):
                load_chunk(n)

            def mod_row(dst, r):
                return sp.dma_start(dst, rows_dram[8 * r:8 * (r + 1), :].rearrange("a b -> (a b)").unsqueeze(0).to_broadcast([P, D]))

            emptied(sp, INDEX[("cb", KT - 1)])
            for v in range(2):
                mod_row(gate1[:, v, :], v).then_inc(s_g1rows, 16)
            for n in range(30, len(CHUNK_LIST)):
                load_chunk(n)
            job_done(sp, "at", KT - 1)
            for s in range(2):
                for v in range(2):
                    mod_row(mod2[:, s, v, :], 2 * (s + 1) + v).then_inc(s_m2rows, 16)

            def load_gate_up(e, b):
                for j, w in enumerate((io["w1"], io["w3"])):
                    sp.dma_start(slot[2 * b + j].rearrange("p (k n) -> p k n", k=KT), up_src(w, e)).then_inc(s_wgu[b], 16)

            def load_down(e, b):
                sp.dma_start(down[b].rearrange("p (k n) -> p k n", k=4), down_src(e)).then_inc(s_wd[b], 16)

            job_done(sp, "wo", 2 * NT - 1)
            load_gate_up(0, 0)
            load_gate_up(1, 1)
            load_down(0, 0)
            emptied(sp, INDEX[("wo", 2 * NT - 1)])
            load_down(1, 1)
            for i in range(NT):
                sp.wait_ge(s_h2, i + 1)
                sp.dma_start(h2_dram[P * i:P * (i + 1), :], h2[:, i, :]).then_inc(s_h2out, 16)
            sp.wait_ge(s_h2out, 16 * NT)
            job_done(sp, "h2T", NT - 1)
            for v in range(2):
                mod_row(gate2[:, v, :], 6 + v).then_inc(s_g2rows, 16)
            sp.wait_ge(s_tab, 16 * 2 * NT)
            sp.dma_start(idxp[:, :], table_dram).then_inc(s_idx, 16)
            with sp.Fori(0, (EXPERTS - 2) // 2) as it:
                for b in range(2):
                    sp.wait_ge(s_gu, 2 * it + b + 1)
                    load_gate_up(2 * it + b + 2, b)
                    sp.wait_ge(s_d, 2 * it + b + 1)
                    load_down(2 * it + b + 2, b)

            def more(e, c, k):
                sp.wait_ge(s_d, k + EXPERTS)
                for j, w in enumerate((io["w1"], io["w3"])):
                    sp.dma_start(slot[j].rearrange("p (k n) -> p k n", k=KT), up_src(w, e)).then_inc(s_ofw, 16)
                sp.dma_start(down[0].rearrange("p (k n) -> p k n", k=4), down_src(e)).then_inc(s_ofw, 16)

            more_chunks(sp, more)
            job = sp.value_load(meta[0:1, 32:33], min_val=0, max_val=EXPERTS * CHUNKS)
            for b in range(2):
                sp.wait_ge(s_yst[b], 16 * EXPERTS // 2)
            with sp.If(job > 0):
                sp.wait_ge(s_ofst, job)
                sp.sem_inc(s_ofst, 1)
            for i in range(NT):
                for j in range(2):
                    sp.dma_start(yg[2 * i + j], y_dram[T * j + P * i:T * j + P * (i + 1), :]).then_inc(s_yg[i], 16)
            for i in range(NT):
                sp.wait_ge(s_out, i + 1)
                dst = io["y_prompt"] if i == CTX else io["y_sample"][P * i:P * (i + 1), :]
                sp.dma_start(dst, x_sb[:, D * i:D * (i + 1)]).then_inc(s_outx, 16)
            sp.wait_ge(s_outx, 16 * NT)
            sp.wait_ge(s_nk, 16 * GROUPS)
            sp.wait_ge(s_nv, 16 * GROUPS)

        @block.gpsimd
        def _(pool):
            steps = [0]

            def link(ins):
                steps[0] += 1
                ins.then_inc(s_pool, 1)
                pool.wait_ge(s_pool, steps[0])

            nc.gpsimd.memset(ones[:, :], 1.0).then_inc(s_const, 1)
            link(nc.gpsimd.memset(ident[:, :], 0.0))
            nc.gpsimd.affine_select(out=ident[:, :], in_=ident[:, :], compare_op=ALU.not_equal, fill=1.0, base=0,
                                    pattern=[[-1, P]], channel_multiplier=1).then_inc(s_const, 1)
            link(nc.gpsimd.memset(tri[:, :], 0.0))
            nc.gpsimd.affine_select(out=tri[:, :], in_=tri[:, :], compare_op=ALU.is_ge, fill=1.0, base=0,
                                    pattern=[[-1, P]], channel_multiplier=1).then_inc(s_const, 1)
            nc.gpsimd.memset(no_pair[:, :], PAIRS_ALL).then_inc(s_zero, 1)
            pool.wait_ge(s_zero, 1)
            pool.dma_start(table_dram, no_pair[:, :]).then_inc(s_tabz, 16)
            for z in range(2 * NT * GROUPS):
                g, zz = divmod(z, 2 * NT)
                which, i = divmod(zz, NT)
                b = z % 2
                if zz == 0:
                    if g:
                        emptied(pool, INDEX[("kcT", g - 1)])
                        pool.wait_ge(s_pv, 20 * g)
                    pool.dma_start(kc, io["cache_k"][:, GW * g:GW * (g + 1)]).then_inc(s_kc[g], 16)
                    pool.dma_start(v_sb[:, 4, :], io["cache_v"][:, GW * g:GW * (g + 1)]).then_inc(s_vc[g], 16)
                pool.wait_ge(s_zn, z + 1)
                if z >= 2:
                    job_done(pool, "qkT", z - 2)
                if z == 11:
                    pool.wait_ge(s_nk, 16)
                if i == CTX:
                    g_row = row("qg" if which == 0 else "kg")
                    nc.gpsimd.tensor_tensor(qk_r[b].rearrange("p (s d) -> p s d", d=QK), qk_n[b].rearrange("p (s d) -> p s d", d=QK),
                                            g_row.unsqueeze(1).to_broadcast([P, 8, QK]), mult).then_inc(s_zr, 1)
                    if which == 1:
                        pool.wait_ge(s_zr, z + 1)
                        pool.dma_start(io["new_k"][:, GW * g:GW * (g + 1)], qk_r[b]).then_inc(s_nk, 16)
                    continue
                src = qk_n[b].rearrange("p (s x a f) -> p s x a f", s=8, x=2, a=2)
                dst = qk_r[b].rearrange("p (s x a f) -> p s x a f", s=8, x=2, a=2)
                sin = ropeS[:, 256 * which + 64 * i:256 * which + 64 * (i + 1)].rearrange("p (x a f) -> p x a f", x=2, a=2)
                nc.gpsimd.tensor_tensor(dst[:, :, :, 0, :], src[:, :, :, 1, :], sin[:, :, 0, :].unsqueeze(1).to_broadcast([P, 8, 2, 16]), mult)
                link(nc.gpsimd.tensor_tensor(dst[:, :, :, 1, :], src[:, :, :, 0, :], sin[:, :, 1, :].unsqueeze(1).to_broadcast([P, 8, 2, 16]), mult))
                pool.wait_ge(s_m1, z + 1 - (z // 5))
                nc.gpsimd.tensor_tensor(qk_r[b], qk_r[b], qk_s[b], add).then_inc(s_zr, 1)
            for i in range(NT):
                pool.wait_ge(s_h2m, i + 1)
                nc.gpsimd.tensor_tensor(h2[:, i, :], h2[:, i, :], mod2[:, 1, int(i == CTX), :], add).then_inc(s_h2, 1)
            link(nc.gpsimd.iota(pair_ids[:, :], pattern=[[P, 2 * NT]], base=0, channel_multiplier=1))
            pool.wait_ge(s_pos, 1)
            pool.wait_ge(s_tabz, 16)
            for j in range(2 * NT):
                nc.gpsimd.indirect_dma_start(table_rows, bass.IndirectOffsetOnAxis(ap=pos[:, j:j + 1], axis=0),
                                             pair_ids[:, j:j + 1], None).then_inc(s_tab, 16)

            def gather(b, index, signal):
                nc.gpsimd.indirect_dma_start(xg[b], None, h2_dram, bass.IndirectOffsetOnAxis(ap=index, axis=0)).then_inc(signal, 16)

            def scatter(b, index, signal):
                nc.gpsimd.indirect_dma_start(y_dram, bass.IndirectOffsetOnAxis(ap=index, axis=0), ys[b], None,
                                             bounds_check=PAIRS_ALL - 1, oob_is_err=False).then_inc(signal, 16)

            pool.wait_ge(s_slot, 1)
            pool.wait_ge(s_h2out, 16 * NT)
            for e in range(XG):
                gather(e, idx[:, e * CHUNKS:e * CHUNKS + 1], s_xg[e])
            for e in range(EXPERTS):
                if e + XG < EXPERTS:
                    pool.wait_ge(s_T, e + 1)
                    gather(e % XG, idx[:, (e + XG) * CHUNKS:(e + XG) * CHUNKS + 1], s_xg[e % XG])
                pool.wait_ge(s_ydve, e + 1)
                pool.wait_ge(s_yact, e + 1)
                scatter(e % 2, idxp[:, e * CHUNKS:e * CHUNKS + 1], s_yst[e % 2])
            copies = steps[0]

            def more(e, c, k):
                pool.wait_ge(s_T, k + EXPERTS)
                pool.wait_ge(s_yst[1], 16 * EXPERTS // 2)
                nc.gpsimd.tensor_copy(idxc[:, 0:1], idx[:, bass.ds(e * CHUNKS + c, 1)])
                nc.gpsimd.tensor_copy(idxc[:, 1:2], idxp[:, bass.ds(e * CHUNKS + c, 1)]).then_inc(s_pool, 1)
                pool.wait_ge(s_pool, k + (copies + 1))
                nc.gpsimd.tensor_tensor(unused[:, 0:1], ones[:, 0:1], ones[:, 0:1], mult)
                gather(0, idxc[:, 0:1], s_ofx)
                pool.wait_ge(s_ydve, k + EXPERTS + 1)
                nc.gpsimd.tensor_tensor(unused[:, 0:1], ones[:, 0:1], ones[:, 0:1], mult)
                pool.wait_ge(s_yact, k + EXPERTS + 1)
                nc.gpsimd.tensor_tensor(unused[:, 0:1], ones[:, 0:1], ones[:, 0:1], mult)
                scatter(0, idxc[:, 1:2], s_ofy)
                pool.wait_ge(s_ofy, k * 16 + 16)
                pool.sem_inc(s_ofst, 1)

            more_chunks(pool, more)

        @block.scalar
        def _(act):
            A = nc.scalar.activation

            def evict(kind, n, out, in_, func=ACT.Copy):
                job_done(act, kind, n)
                return A(out, in_, func).then_inc(s_emptied["act"], 1)

            def ada_copy(n):
                if n >= 2:
                    job_done(act, "adaT", n - 2)
                evict("ada", n, ada_rows[n % 2][:, :], job_psum("ada", n)[0:2, 0:512])

            act.wait_ge(s_cols, 16)
            A(silu_c[:, :], col("cT"), ACT.Silu).then_inc(s_siluc, 1)
            act.wait_ge(s_x, 32)
            for i in range(NT):
                A(xn[:, i, :], x_sb[:, D * i:D * (i + 1)], ACT.Square, accum_out=stat[:, i:i + 1]).then_inc(s_xss, 1)
            act.wait_ge(s_xss, NT)
            act.wait_ge(s_const, 4)
            A(stat[:, NT:2 * NT], stat[:, 0:NT], ACT.Sqrt, bias=eps[:, :], scale=1.0 / D).then_inc(s_xsd, 1)
            act.wait_ge(s_xrs, 1)
            for i in range(NT):
                A(xn[:, i, :], x_sb[:, D * i:D * (i + 1)], ACT.Copy, scale=stat[:, 2 * NT + i:2 * NT + i + 1]).then_inc(s_xn, 1)
            for n in range(4):
                ada_copy(n)
            act.wait_ge(s_mod1, 1)


            for k in range(1, KT, 2):
                job_done(act, "xT", k)
                for v, (lo, hi) in enumerate(((0, N_LAT), (N_LAT, T))):
                    last = A(hT[:, k, lo:hi], job_psum("xT", k)[:, lo:hi], ACT.Identity, bias=mod[:, 2 * k + v:2 * k + v + 1],
                             scale=a1[:, 2 * k + v:2 * k + v + 1])
                last.then_inc(s_emptied["act"], 1)
            act.wait_ge(s_lamx, 1)
            A(neglam[:, 2:4], neglam[:, 0:2], ACT.Exp).then_inc(s_lame, 1)

            def qk_stats(z):
                b = z % 2
                job_done(act, "qk", z)
                if z >= 2:
                    act.wait_ge(s_zr, z - 1)
                A(qk_s[b], job_psum("qk", z)[:, 0:512], ACT.Square).then_inc(s_sq, 1)
                act.wait_ge(s_ss, z + 1)
                A(qkstat[:, 16 * b + 8:16 * b + 16], qkstat[:, 16 * b:16 * b + 8], ACT.Sqrt, bias=eps[:, :], scale=1.0 / QK).then_inc(s_sd, 1)

            def qkT_copy(z):
                g, zz = divmod(z, 2 * NT)
                which, i = divmod(zz, NT)
                src = job_psum("qkT", z)[:, 0:GW].rearrange("p (h t) -> p h t", h=GROUP_HEADS)
                if which == 0:
                    dst = qT[:, :, P * i:P * (i + 1)]
                else:
                    off = P * i if i < CTX else KEYS
                    dst = kT[:, :, off:off + P]
                evict("qkT", z, dst, src)

            for g in range(GROUPS):
                for zz in range(2 * NT):
                    qk_stats(2 * NT * g + zz)
                    if zz:
                        qkT_copy(2 * NT * g + zz - 1)

                def v_copy(i):
                    if i == CTX and g:
                        act.wait_ge(s_nv, 16 * g)
                    ins = evict("v", NT * g + i, v_sb[:, i if i < CTX else 5, :], job_psum("v", NT * g + i)[:, 0:GW])
                    return ins

                v_copy(0)
                qkT_copy(2 * NT * g + 2 * NT - 1)
                evict("kcT", g, kT[:, :, N_LAT:KEYS], job_psum("kcT", g)[:, 0:GW].rearrange("p (h t) -> p h t", h=GROUP_HEADS))
                for i in range(1, NT):
                    v_copy(i)
                for n in range(4):
                    ada_copy(4 + 4 * g + n)
                emptied(act, INDEX[("v", NT * g + CTX)])
                act.dma_start(io["new_v"][:, GW * g:GW * (g + 1)], v_sb[:, 5, :]).then_inc(s_nv, 16)

                def probs_T(n):
                    i = n % NT
                    act.wait_ge(s_aTp, n + 1)
                    if n - 20 * g >= 2:
                        act.wait_ge(s_pv, n - 1)
                    w = KEYS if i < CTX else N_CTX
                    A(aT[n % 2][:, 0:w], psum[:, 3072:3072 + w], ACT.Copy).then_inc(s_aT, 1)

                items = 20
                for m in range(items + 2):
                    n = items * g + m
                    if m >= 2:
                        probs_T(n - 2)
                    if m < items:
                        i = n % NT
                        w = KEYS if i < CTX else N_CTX
                        act.wait_ge(s_max, n + 1)
                        if n >= 2:
                            act.wait_ge(s_mix, n - 1)
                        S = psum[:, 1536 * (n % 2):1536 * (n % 2 + 1)]
                        st = sm[:, 8 * (n % 2):8 * (n % 2) + 8]
                        for c in range(2):
                            last = A(prob[n % 2][:, c, 0:w], S[:, 896 * c:896 * c + w], ACT.Exp, bias=st[:, 2 + c:3 + c],
                                     scale=SM_SCALE, accum_out=st[:, 4 + c:5 + c])
                        last.then_inc(s_exp, 1)

            evict("rowsT", 0, rowpackT[:, :], job_psum("rowsT", 0)[0:64, 0:P])
            act.wait_ge(s_emptied["act"], EMPTIED[INDEX[("rowsT", 0)]][1])
            act.sem_inc(s_rowsT, 1)
            act.wait_ge(s_oss, 1)
            A(ostat[:, 40:80], ostat[:, 0:40], ACT.Sqrt, bias=eps[:, :], scale=1.0 / P).then_inc(s_osd, 1)
            for n in range(KT):
                if n >= 2:
                    job_done(act, "cb", n - 2)
                    emptied(act, INDEX[("cx", n - 2)])
                evict("cc", n, t_cc[n % 2], job_psum("cc", n)[:, 0:T])
            for j in range(2 * NT):
                i, half = divmod(j, 2)
                job_done(act, "oT", j)
                A(oT[:, 4 * half:4 * half + 4, P * i:P * (i + 1)], job_psum("oT", j)[:, 0:512].rearrange("p (h t) -> p h t", h=4),
                  ACT.Copy, scale=rowpack[:, 0:1]).then_inc(s_emptied["act"], 1)
            for n in range(KT):
                if n >= 1:
                    emptied(act, INDEX[("cv", n - 1)])
                evict("gc", n, t_gc, job_psum("gc", n)[:, 0:T], ACT.Sigmoid)
                if n >= 1:
                    emptied(act, INDEX[("at", n - 1)])
                evict("ga", n, t_ga, job_psum("ga", n)[:, 0:T], ACT.Sigmoid)
            for i in range(NT):
                act.wait_ge(s_x2, 2 * NT if i == CTX else 2 * NT)
                A(h2[:, i, :], x_sb[:, D * i:D * (i + 1)], ACT.Square, accum_out=stat[:, i:i + 1]).then_inc(s_x2ss, 1)
            act.wait_ge(s_x2ss, NT)
            A(stat[:, NT:2 * NT], stat[:, 0:NT], ACT.Sqrt, bias=eps[:, :], scale=1.0 / D).then_inc(s_x2sd, 1)
            for i in range(NT):
                evict("h2T", i, h2T[:, i, :, :], job_psum("h2T", i).rearrange("p (k t) -> p k t", k=KT))
            act.wait_ge(s_rexp_in, 1)
            A(rt[:, 300:320], rt[:, 280:300], ACT.Exp)
            A(rt[:, 325:330], rt[:, 320:325], ACT.Exp).then_inc(s_rexp, 1)

            def tokens_T(k):
                act.wait_ge(s_T, k + 1)
                A(xgT.rearrange("p k s -> p (k s)"), psum[:, 0:1024], ACT.Copy).then_inc(s_xgT, 1)

            def gate(k):
                act.wait_ge(s_gu, k + 1)
                A(sg, psum[:, 1024:1536], ACT.Silu).then_inc(s_sg, 1)

            def hidden_T(k):
                act.wait_ge(s_HT, k + 1)
                A(hhT.rearrange("p k s -> p (k s)"), psum[:, 2048:2560], ACT.Copy).then_inc(s_hhT, 1)

            def y_right(k, b):
                act.wait_ge(s_d, k + 1)
                A(ys[b][:, 512:1024], psum[:, 3072:3584], ACT.Copy).then_inc(s_yact, 1)

            tokens_T(0)
            gate(0)
            tokens_T(1)
            hidden_T(0)
            for e in (1, 2):
                gate(e)
                tokens_T(e + 1)
                y_right(e - 1, (e - 1) % 2)
                hidden_T(e)
            with act.Fori(0, 6) as it:
                for j in range(2):
                    e = 2 * it + 3 + j
                    gate(e)
                    tokens_T(e + 1)
                    act.wait_ge(s_yst[j], it * 16 + 16)
                    y_right(e - 1, j)
                    hidden_T(e)
            gate(15)
            act.wait_ge(s_yst[0], 16 * 7)
            y_right(14, 0)
            hidden_T(15)
            act.wait_ge(s_yst[1], 16 * 7)
            y_right(15, 1)
            act.wait_ge(s_yst[0], 16 * 8)

            def more(e, c, k):
                tokens_T(k + EXPERTS)
                gate(k + EXPERTS)
                hidden_T(k + EXPERTS)
                y_right(k + EXPERTS, 0)

            more_chunks(act, more)

        @block.vector
        def _(dve):
            V = nc.vector
            steps = [0]

            def link(ins):
                steps[0] += 1
                ins.then_inc(s_dve, 1)
                dve.wait_ge(s_dve, steps[0])

            V.memset(eps[:, :], EPS).then_inc(s_const, 1)
            dve.wait_ge(s_xsd, 1)
            V.reciprocal(stat[:, 2 * NT:3 * NT], stat[:, NT:2 * NT]).then_inc(s_xrs, 1)

            def ada_copy(n):
                job_done(dve, "adaT", n)
                V.tensor_tensor(mod[:, 8 * n:8 * n + 8].rearrange("p (n v) -> p n v", v=2),
                                job_psum("adaT", n)[:, 0:8].rearrange("p (n v) -> p n v", v=2),
                                col("b_ada")[:, 4 * n:4 * n + 4].unsqueeze(2).to_broadcast([P, 4, 2]), add).then_inc(s_emptied["dve"], 1)

            for n in range(4):
                ada_copy(n)
            emptied(dve, INDEX[("adaT", 3)])
            V.scalar_tensor_tensor(out=a1[:, :].rearrange("p (k v) -> p k v", v=2), in0=mod[:, 16:32].rearrange("p (k v) -> p k v", v=2),
                                   scalar=1.0, in1=col("g1").unsqueeze(2).to_broadcast([P, KT, 2]), op0=add, op1=mult).then_inc(s_mod1, 1)
            dve.wait_ge(s_mod1, 1)
            for k in range(0, KT, 2):
                job_done(dve, "xT", k)
                for v, (lo, hi) in enumerate(((0, N_LAT), (N_LAT, T))):
                    last = V.tensor_scalar(hT[:, k, lo:hi], job_psum("xT", k)[:, lo:hi], a1[:, 2 * k + v:2 * k + v + 1],
                                           mod[:, 2 * k + v:2 * k + v + 1], mult, add)
                last.then_inc(s_emptied["dve"], 1)
            dve.wait_ge(s_rows, 16)
            lamrow = row("lam").rearrange("p (a b n) -> p a b n", a=2, b=2)
            link(V.tensor_tensor(qk_s[0][:, 0:128].rearrange("p (a n) -> p a n", a=2), lamrow[:, :, 0, :], lamrow[:, :, 1, :], mult))
            V.reduce_sum(neglam[:, 0:2], qk_s[0][:, 0:128].rearrange("p (a n) -> p a n", a=2), axis=AX).then_inc(s_lamx, 1)
            dve.wait_ge(s_rope, 16)
            C = ropet[:, 0:256].rearrange("p (i d) -> p i d", i=4)
            S = ropet[:, 256:512].rearrange("p (i x a f) -> p i x a f", i=4, x=2, a=2)
            for w, name in enumerate(("qg", "kg")):
                g = row(name)
                V.tensor_tensor(ropeC[:, 256 * w:256 * (w + 1)].rearrange("p (i d) -> p i d", i=4), C,
                                g.unsqueeze(1).to_broadcast([P, 4, QK]), mult)
                gs = g.rearrange("p (x a f) -> p x a f", x=2, a=2)
                out = ropeS[:, 256 * w:256 * (w + 1)].rearrange("p (i x a f) -> p i x a f", i=4, x=2, a=2)
                for a in range(2):
                    last = V.tensor_tensor(out[:, :, :, a, :], S[:, :, :, a, :], gs[:, :, 1 - a, :].unsqueeze(1).to_broadcast([P, 4, 2, 16]), mult)
            link(last)
            dve.wait_ge(s_lame, 1)
            link(V.tensor_tensor(neglam[:, 4:5], neglam[:, 3:4], neglam[:, 2:3], sub))
            link(V.tensor_scalar(neglam[:, 5:6], neglam[:, 4:5], -LAM_INIT, None, add))
            nl = neglam[:, 5:6]

            def qk_norm(z):
                g, zz = divmod(z, 2 * NT)
                which, i = divmod(zz, NT)
                b = z % 2
                ss, sd, rs = (qkstat[:, 16 * b:16 * b + 8], qkstat[:, 16 * b + 8:16 * b + 16], qkstat[:, 16 * b:16 * b + 8])
                dve.wait_ge(s_sq, z + 1)
                V.reduce_sum(ss, qk_s[b].rearrange("p (s d) -> p s d", d=QK), axis=AX).then_inc(s_ss, 1)
                dve.wait_ge(s_sd, z + 1)
                link(V.reciprocal(rs, sd))
                if z >= 2:
                    dve.wait_ge(s_zr, z - 1)
                ins = V.tensor_tensor(qk_n[b].rearrange("p (s d) -> p s d", d=QK), job_psum("qk", z)[:, 0:512].rearrange("p (s d) -> p s d", d=QK),
                                      rs.unsqueeze(2).to_broadcast([P, 8, QK]), mult)
                ins.then_inc(s_emptied["dve"], 1)
                emptied(dve, INDEX[("qk", z)])
                if i < CTX:
                    V.tensor_tensor(qk_s[b].rearrange("p (s d) -> p s d", d=QK), qk_n[b].rearrange("p (s d) -> p s d", d=QK),
                                    ropeC[:, 256 * which + 64 * i:256 * which + 64 * (i + 1)].unsqueeze(1).to_broadcast([P, 8, QK]),
                                    mult).then_inc(s_m1, 1)
                dve.sem_inc(s_zn, 1)

            items = 20
            for g in range(GROUPS):
                for zz in range(2 * NT):
                    qk_norm(2 * NT * g + zz)
                for n in range(4):
                    ada_copy(4 + 4 * g + n)

                def o_copy(n):
                    h, i = divmod(n, NT)
                    dve.wait_ge(s_pv, n + 1)
                    V.tensor_copy(o_tok[:, i, P * h:P * (h + 1)], psum[:, 3840:3968]).then_inc(s_o, 1)

                def mix(n):
                    i = n % NT
                    w = KEYS if i < CTX else N_CTX
                    st = sm[:, 8 * (n % 2):8 * (n % 2) + 8]
                    dve.wait_ge(s_exp, n + 1)
                    link(V.reciprocal(st[:, 6:8], st[:, 4:6]))
                    link(V.tensor_scalar(st[:, 7:8], st[:, 7:8], nl, None, mult))
                    if n - 20 * g >= 2:
                        dve.wait_ge(s_aTp, n - 1)
                    link(V.tensor_scalar(prob[n % 2][:, 1, 0:w], prob[n % 2][:, 1, 0:w], st[:, 7:8], None, mult))
                    V.scalar_tensor_tensor(out=amix[n % 2][:, 0:w], in0=prob[n % 2][:, 0, 0:w], scalar=st[:, 6:7],
                                           in1=prob[n % 2][:, 1, 0:w], op0=mult, op1=add).then_inc(s_mix, 1)

                for m in range(items + 3):
                    n = items * g + m
                    if m >= 3:
                        o_copy(n - 3)
                    if m < items:
                        i = n % NT
                        w = KEYS if i < CTX else N_CTX
                        base = 1536 * (n % 2)
                        st = sm[:, 8 * (n % 2):8 * (n % 2) + 8]
                        dve.wait_ge(s_scores, n + 1)
                        S2 = psum[:, base:base + 1792].rearrange("p (c k) -> p c k", c=2)[:, :, 0:w]
                        link(V.reduce_max(st[:, 0:2], S2, axis=AX))
                        V.tensor_scalar(st[:, 2:4], st[:, 0:2], -SM_SCALE, None, mult).then_inc(s_max, 1)
                    if 1 <= m <= items:
                        mix(n - 1)
            emptied(dve, INDEX[("adaT", 11)])
            m6 = mod[:, :].rearrange("p (s k v) -> p s v k", s=6, v=2)
            rp = rowpack[:, :].rearrange("p (s v k) -> p s v k", s=4, v=2)
            V.tensor_copy(rp[:, 0], m6[:, 2])
            V.scalar_tensor_tensor(out=rp[:, 1], in0=m6[:, 4], scalar=1.0, in1=col("g2").unsqueeze(1).to_broadcast([P, 2, KT]), op0=add, op1=mult)
            V.tensor_copy(rp[:, 2], m6[:, 3])
            V.tensor_copy(rp[:, 3], m6[:, 5]).then_inc(s_rowpack, 1)
            emptied(dve, INDEX[("v", NT * GROUPS - 1)])
            for i in range(NT):
                for half in range(2):
                    tmp = qk_s[half]
                    o_v = o_tok[:, i, 512 * half:512 * (half + 1)]
                    link(V.tensor_tensor(tmp, o_v, o_v, mult))
                    last = V.reduce_sum(ostat[:, 8 * i + 4 * half:8 * i + 4 * half + 4], tmp.rearrange("p (h n) -> p h n", h=4), axis=AX)
            last.then_inc(s_oss, 1)
            dve.wait_ge(s_osd, 1)
            link(V.reciprocal(ostat[:, 0:40], ostat[:, 40:80]))
            for i in range(NT):
                ov = o_tok[:, i, :].rearrange("p (h n) -> p h n", h=HEADS)
                V.tensor_tensor(ov, ov, ostat[:, 8 * i:8 * i + 8].unsqueeze(2).to_broadcast([P, HEADS, P]), mult).then_inc(s_on, 1)
            job_done(dve, "rowsT", 0)
            link(V.tensor_scalar(rowpack[:, 0:1], col("subln"), 1.0 - LAM_INIT, None, mult))

            def pads():
                for b in range(2):
                    for c in (0, N_LAT + 1, N_LAT + 2, T + 3):
                        last = V.memset(t_m[b][:, c:c + 1], 0.0)
                return last

            dve.wait_ge(s_nk, 16 * GROUPS)
            dve.wait_ge(s_nv, 16 * GROUPS)
            link(pads())
            w = col("conv")
            for n in range(KT):
                b = n % 2
                emptied(dve, INDEX[("cc", n)])
                job_done(dve, "cx", n)
                ps = job_psum("cx", n)
                V.tensor_tensor(t_m[b][:, 1:N_LAT + 1], ps[:, 0:N_LAT], t_cc[b][:, 0:N_LAT], mult)
                V.tensor_tensor(t_m[b][:, N_LAT + 3:T + 3], ps[:, N_LAT:T], t_cc[b][:, N_LAT:T], mult).then_inc(s_emptied["dve"], 1)
                emptied(dve, INDEX[("cx", n)])
                link(V.tensor_scalar(t_cv[b], t_m[b][:, 1:643], w[:, 8 + n:9 + n], None, mult))
                link(V.scalar_tensor_tensor(out=t_cv[b], in0=t_m[b][:, 0:642], scalar=w[:, n:n + 1], in1=t_cv[b], op0=mult, op1=add))
                link(V.scalar_tensor_tensor(out=t_cv[b], in0=t_m[b][:, 2:644], scalar=w[:, 16 + n:17 + n], in1=t_cv[b], op0=mult, op1=add))
                job_done(dve, "cb", n)
                ps = job_psum("cb", n)
                V.tensor_tensor(uT[:, n, 0:N_LAT], ps[:, 0:N_LAT], t_cv[b][:, 0:N_LAT], mult)
                V.tensor_tensor(uT[:, n, N_LAT:T], ps[:, N_LAT:T], t_cv[b][:, N_LAT + 2:T + 2], mult).then_inc(s_emptied["dve"], 1)
            for n in range(KT):
                emptied(dve, INDEX[("gc", n)])
                job_done(dve, "cv", n)
                V.tensor_tensor(mixT[:, n, :], job_psum("cv", n)[:, 0:T], t_gc, mult).then_inc(s_emptied["dve"], 1)
                emptied(dve, INDEX[("ga", n)])
                if n:
                    dve.wait_ge(s_mixT, n)
                job_done(dve, "at", n)
                V.tensor_tensor(t_at, job_psum("at", n)[:, 0:T], t_ga, mult).then_inc(s_emptied["dve"], 1)
                emptied(dve, INDEX[("at", n)])
                V.tensor_tensor(mixT[:, n, :], mixT[:, n, :], t_at, add).then_inc(s_mixT, 1)
            dve.wait_ge(s_g1rows, 32)
            for j in range(2 * NT):
                n, i = divmod(j, NT)
                v = int(i == CTX)
                if j:
                    dve.wait_ge(s_x2, j)
                job_done(dve, "wo", j)
                V.tensor_tensor(t_wo, job_psum("wo", j)[:, 0:512], gate1[:, v, 512 * n:512 * (n + 1)], mult).then_inc(s_emptied["dve"], 1)
                emptied(dve, INDEX[("wo", j)])
                xs = x_sb[:, D * i + 512 * n:D * i + 512 * (n + 1)]
                V.tensor_tensor(xs, xs, t_wo, add).then_inc(s_x2, 1)
            dve.wait_ge(s_x2sd, 1)
            link(V.reciprocal(stat[:, 2 * NT:3 * NT], stat[:, NT:2 * NT]))
            dve.wait_ge(s_m2rows, 64)
            for i in range(NT):
                V.scalar_tensor_tensor(out=h2[:, i, :], in0=x_sb[:, D * i:D * (i + 1)], scalar=stat[:, 2 * NT + i:2 * NT + i + 1],
                                       in1=mod2[:, 0, int(i == CTX), :], op0=mult, op1=mult).then_inc(s_h2m, 1)

            def tile(off, n, k=1):
                t = rt[:, off:off + NT * n * k]
                return t.rearrange("p (i n) -> p i n", i=NT) if k == 1 else t.rearrange("p (i a n) -> p i a n", i=NT, a=k)

            logit = tile(0, 20)
            gl, el = logit[:, :, 0:4], logit[:, :, 4:20].rearrange("p i (g j) -> p i g j", g=4)
            job_done(dve, "route", 0)
            V.tensor_tensor(logit, job_psum("route", 0)[:, 0:100].rearrange("p (i n) -> p i n", i=NT),
                            row("b_route").unsqueeze(1).to_broadcast([P, NT, 20]), add).then_inc(s_emptied["dve"], 1)
            emptied(dve, INDEX[("route", 0)])
            gmax = rt[:, 100:105]
            link(V.reduce_max(gmax, gl, axis=AX))
            desc = row("desc").unsqueeze(1).to_broadcast([P, NT, 4])

            def first_of(out, tmp, tmpmax, values, best):
                link(V.tensor_tensor(tmp, values, best.unsqueeze(2).to_broadcast([P, NT, 4]), ALU.is_equal))
                link(V.tensor_tensor(tmp, tmp, desc, mult))
                link(V.reduce_max(tmpmax, tmp, axis=AX))
                link(V.tensor_tensor(out, tmp, tmpmax.unsqueeze(2).to_broadcast([P, NT, 4]), ALU.is_equal))

            ohg, tmp, tmpmax = tile(110, 4), tile(130, 4), rt[:, 105:110]
            first_of(ohg, tmp, tmpmax, gl, gmax)
            V.tensor_tensor(rt[:, 280:300].rearrange("p (i n) -> p i n", i=NT), gl, gmax.unsqueeze(2).to_broadcast([P, NT, 4]), sub)
            prod = tile(400, 4, 4)
            link(V.tensor_tensor(prod, el, ohg.unsqueeze(3).to_broadcast([P, NT, 4, 4]), mult))
            esel = tile(150, 4)
            link(V.reduce_sum(esel, rt[:, 400:480].rearrange("p (i g j) -> p i j g", i=NT, g=4), axis=AX))
            m1, m2 = rt[:, 170:175], rt[:, 175:180]
            link(V.reduce_max(m1, esel, axis=AX))
            oh1, oh2 = tile(180, 4), tile(200, 4)
            first_of(oh1, tmp, tmpmax, esel, m1)
            e2 = tile(220, 4)
            link(V.scalar_tensor_tensor(out=e2, in0=oh1, scalar=-BIG, in1=esel, op0=mult, op1=add))
            link(V.reduce_max(m2, e2, axis=AX))
            first_of(oh2, tmp, tmpmax, e2, m2)
            V.tensor_tensor(rt[:, 320:325], m2, m1, sub).then_inc(s_rexp_in, 1)
            mask = [rt[:, 500 + 80 * j:580 + 80 * j] for j in range(2)]
            both = rt[:, 660:740]
            for j, oh in enumerate((oh1, oh2)):
                link(V.tensor_tensor(mask[j].rearrange("p (i g j) -> p i g j", i=NT, g=4), ohg.unsqueeze(3).to_broadcast([P, NT, 4, 4]),
                                     oh.unsqueeze(2).to_broadcast([P, NT, 4, 4]), mult))
            V.tensor_tensor(both, mask[0], mask[1], add).then_inc(s_mask, 1)
            dve.wait_ge(s_rexp, 1)
            gsum, ex = rt[:, 330:335], rt[:, 325:330]
            link(V.reduce_sum(gsum, rt[:, 300:320].rearrange("p (i n) -> p i n", i=NT), axis=AX))
            link(V.scalar_tensor_tensor(out=rt[:, 335:340], in0=ex, scalar=1.0, in1=gsum, op0=add, op1=mult))
            link(V.reciprocal(comb[:, 0:NT], rt[:, 335:340]))
            link(V.tensor_tensor(comb[:, NT:2 * NT], comb[:, 0:NT], ex, mult))
            job_done(dve, "rank", 0)
            rank, counts = rt[:, 740:820], rt[:, 820:836]
            V.tensor_copy(rank, job_psum("rank", 0)[:, 0:80])
            V.tensor_copy(counts, job_psum("rank", 0)[:, 80:96]).then_inc(s_emptied["dve"], 1)
            emptied(dve, INDEX[("rank", 0)])
            ranks, places, chunk_no = rt[:, 840:850], rt[:, 850:860], rt[:, 1000:1010]
            for j in range(2):
                m3 = mask[j].rearrange("p (i e) -> p i e", i=NT)
                t80 = rt[:, 400:480]
                link(V.tensor_tensor(t80, mask[j], rank, mult))
                link(V.reduce_sum(ranks[:, NT * j:NT * (j + 1)], t80.rearrange("p (i e) -> p i e", i=NT), axis=AX))
                link(V.tensor_tensor(t80.rearrange("p (i e) -> p i e", i=NT), m3, row("ebase").unsqueeze(1).to_broadcast([P, NT, 16]), mult))
                link(V.reduce_sum(places[:, NT * j:NT * (j + 1)], t80.rearrange("p (i e) -> p i e", i=NT), axis=AX))
            link(V.tensor_scalar(chunk_no, ranks, float(SLOTS), None, ALU.is_ge))
            for c in range(2, CHUNKS):
                link(V.scalar_tensor_tensor(out=chunk_no, in0=ranks, scalar=float(SLOTS * c), in1=chunk_no, op0=ALU.is_ge, op1=add))
            link(V.scalar_tensor_tensor(out=places, in0=ranks, scalar=float(EXPERTS * CHUNKS), in1=places, op0=mult, op1=add))
            link(V.scalar_tensor_tensor(out=places, in0=chunk_no, scalar=1.0 - float(EXPERTS * CHUNKS * SLOTS), in1=places, op0=mult, op1=add))
            V.tensor_copy(pos[:, :], places).then_inc(s_pos, 1)
            over, scan, scan2 = rt[:, 860:876], rt[:, 880:912], rt[:, 920:952]
            link(V.tensor_scalar(over, counts, float(SLOTS), None, ALU.is_gt))
            for c in range(2, CHUNKS):
                link(V.scalar_tensor_tensor(out=over, in0=counts, scalar=float(SLOTS * c), in1=over, op0=ALU.is_gt, op1=add))
            V.memset(scan, 0.0)
            link(V.memset(scan2, 0.0))
            link(V.tensor_copy(scan[:, 16:32], over))
            a, b_ = scan, scan2
            for d in (1, 2, 4, 8):
                link(V.tensor_tensor(b_[:, 16:32], a[:, 16:32], a[:, 16 - d:32 - d], add))
                a, b_ = b_, a
            link(V.tensor_copy(meta[:, 0:16], counts))
            link(V.tensor_copy(meta[:, 16:32], a[:, 15:31]))
            V.tensor_copy(meta[:, 32:33], a[:, 31:32]).then_inc(s_meta, 1)

            dve.wait_ge(s_idx, 16)
            pidf, tokf = rt[:, 1100:1180], rt[:, 1180:1260]
            link(V.tensor_copy(pidf, idxp[:, :]))
            link(V.tensor_scalar(tokf, pidf, float(T), -float(T), ALU.is_ge, mult))
            link(V.tensor_tensor(tokf, tokf, pidf, add))
            link(V.tensor_scalar(pidf, pidf, float(PAIRS_ALL), -float(T), ALU.is_ge, mult))
            link(V.tensor_tensor(tokf, tokf, pidf, add))
            V.tensor_copy(idx[:, :], tokf).then_inc(s_slot, 1)

            def hidden(k):
                dve.wait_ge(s_sg, k + 1)
                V.tensor_tensor(hh, psum[:, 1536:2048], sg, mult).then_inc(s_hh, 1)

            def y_left(k, b):
                dve.wait_ge(s_d, k + 1)
                V.tensor_copy(ys[b][:, 0:512], psum[:, 2560:3072]).then_inc(s_ydve, 1)

            hidden(0)
            for e in (1, 2):
                y_left(e - 1, (e - 1) % 2)
                hidden(e)
            with dve.Fori(0, 6) as it:
                for j in range(2):
                    e = 2 * it + 3 + j
                    dve.wait_ge(s_yst[j], it * 16 + 16)
                    y_left(e - 1, j)
                    hidden(e)
            dve.wait_ge(s_yst[0], 16 * 7)
            y_left(14, 0)
            hidden(15)
            dve.wait_ge(s_yst[1], 16 * 7)
            y_left(15, 1)
            dve.wait_ge(s_yst[0], 16 * 8)

            def more(e, c, k):
                hidden(k + EXPERTS)
                y_left(k + EXPERTS, 0)

            more_chunks(dve, more)
            dve.wait_ge(s_g2rows, 32)
            for i in range(NT):
                v = int(i == CTX)
                dve.wait_ge(s_yg[i], 32)
                y1, y2 = yg[2 * i], yg[2 * i + 1]
                link(V.tensor_scalar(y1, y1, comb[:, i:i + 1], None, mult))
                link(V.scalar_tensor_tensor(out=y1, in0=y2, scalar=comb[:, NT + i:NT + i + 1], in1=y1, op0=mult, op1=add))
                link(V.tensor_tensor(y1, y1, gate2[:, v, :], mult))
                xs = x_sb[:, D * i:D * (i + 1)]
                V.tensor_tensor(xs, xs, y1, add).then_inc(s_out, 1)

        @block.tensor
        def _(pe):
            mm, tr = nc.tensor.matmul, nc.tensor.transpose

            def open_job(kind, n):
                j = INDEX[(kind, n)]
                if j >= PAIRS:
                    emptied(pe, j - PAIRS)
                return pair[j % PAIRS]

            def chunk(name):
                n = CHUNK[name]
                pe.wait_ge(s_w[n % W_SLOTS], 16 * (n // W_SLOTS + 1))
                return slot[n % W_SLOTS].rearrange("p (k n) -> p k n", k=KT)

            pe.wait_ge(s_const, 4)
            pe.wait_ge(s_siluc, 1)
            sc = silu_c[:, :].rearrange("p (k v) -> p k v", v=2)

            def ada(n):
                ps = open_job("ada", n)
                w = chunk(("ada", n))
                for k in range(KT):
                    last = mm(ps[0:2, 0:512], sc[:, k, :], w[:, k, :], start=(k == 0), stop=(k == KT - 1))
                last.then_inc(s_job, 1)

            def ada_T(n):
                ps = open_job("adaT", n)
                emptied(pe, INDEX[("ada", n)])
                for t in range(4):
                    last = tr(ps[:, 2 * t:2 * t + 2], ada_rows[n % 2][:, P * t:P * (t + 1)], ident[0:2, 0:2])
                last.then_inc(s_job, 1)

            def ada_all(lo):
                for n in range(lo, lo + 4):
                    ada(n)
                    if n > lo:
                        ada_T(n - 1)
                ada_T(lo + 3)

            ada_all(0)
            pe.wait_ge(s_xn, NT)
            for k in range(KT):
                ps = open_job("xT", k)
                for i in range(NT):
                    last = tr(ps[:, P * i:P * (i + 1)], xn[:, i, P * k:P * (k + 1)], ident[:, :])
                last.then_inc(s_job, 1)
            for k in range(KT):
                emptied(pe, INDEX[("xT", k)])

            def tok_job(kind, n, w, i):
                ps = open_job(kind, n)
                for k in range(KT):
                    last = mm(ps[:, 0:512], hT[:, k, P * i:P * (i + 1)], w[:, k, :], start=(k == 0), stop=(k == KT - 1))
                last.then_inc(s_job, 1)

            def qk_T(z):
                ps = open_job("qkT", z)
                pe.wait_ge(s_zr, z + 1)
                for h in range(GROUP_HEADS):
                    last = tr(ps[:, P * h:P * (h + 1)], qk_r[z % 2][:, P * h:P * (h + 1)], ident[:, :])
                last.then_inc(s_job, 1)

            items = 20
            for g in range(GROUPS):
                for zz in range(2 * NT):
                    which, i = divmod(zz, NT)
                    w = chunk(("in", 6 + 2 * which + g))
                    z = 2 * NT * g + zz
                    tok_job("qk", z, w, i)
                    if zz:
                        qk_T(z - 1)
                w = chunk(("in", 10 + g))
                tok_job("v", NT * g, w, 0)
                qk_T(2 * NT * g + 2 * NT - 1)
                ps = open_job("kcT", g)
                pe.wait_ge(s_kc[g], 16)
                for h in range(GROUP_HEADS):
                    last = tr(ps[:, P * h:P * (h + 1)], kc[:, P * h:P * (h + 1)], ident[:, :])
                last.then_inc(s_job, 1)
                for i in range(1, NT):
                    tok_job("v", NT * g + i, w, i)
                ada_all(4 + 4 * g)
                for n in range(4):
                    emptied(pe, INDEX[("adaT", 7 + 4 * g)] - n)
                pe.wait_ge(s_vc[g], 16)

                def scores(n, c):
                    m = n - items * g
                    h, i = divmod(m, NT)
                    if n >= 2 and c == 0:
                        pe.wait_ge(s_exp, n - 1)
                    if c == 1:
                        pe.wait_ge(s_half, n + 1)
                    base = 1536 * (n % 2) + 896 * c
                    q = qT[64 * c:64 * (c + 1), h, P * i:P * (i + 1)]
                    if i == CTX:
                        parts = ((0, N_CTX, KEYS),)
                    elif c == 0:
                        parts = ((0, 512, 0), (512, 640, 512))
                    else:
                        parts = ((0, 128, 0), (128, 640, 128))
                    for lo, hi, key in parts:
                        last = mm(psum[:, base + lo:base + hi], q, kT[64 * c:64 * (c + 1), h, key:key + hi - lo], start=True, stop=True)
                    last.then_inc(s_half if c == 0 else s_scores, 1)

                for n in range(3):
                    scores(items * g + n, 0)
                    scores(items * g + n, 1)
                for m in range(items):
                    n = items * g + m
                    h, i = divmod(m, NT)
                    tiles = range(NT) if i < CTX else range(1)
                    pe.wait_ge(s_mix, n + 1)
                    if m >= 1:
                        pe.wait_ge(s_o, n)
                    for j in tiles:
                        last = tr(psum[:, 3072 + P * j:3072 + P * (j + 1)], amix[n % 2][:, P * j:P * (j + 1)], ident[:, :])
                    last.then_inc(s_aTp, 1)
                    if m + 3 < items:
                        scores(n + 3, 0)
                    pe.wait_ge(s_aT, n + 1)
                    for j in tiles:
                        vt = v_sb[:, j if i < CTX else 5, P * h:P * (h + 1)]
                        last = mm(psum[:, 3840:3968], aT[n % 2][:, P * j:P * (j + 1)], vt, start=(j == 0), stop=(j == len(tiles) - 1))
                    last.then_inc(s_pv, 1)
                    if m + 3 < items:
                        scores(n + 3, 1)
                pe.wait_ge(s_o, items * (g + 1))

            ps = open_job("rowsT", 0)
            pe.wait_ge(s_rowpack, 1)
            tr(ps[0:64, 0:P], rowpack[:, :], ident[:, :]).then_inc(s_job, 1)

            def feat_job(kind, n, w, src):
                ps = open_job(kind, n)
                for lo, hi in ((0, N_LAT), (N_LAT, T)):
                    for k in range(KT):
                        last = mm(ps[:, lo:hi], w[:, k, P * (n % 4):P * (n % 4 + 1)], src[:, k, lo:hi], start=(k == 0), stop=(k == KT - 1))
                last.then_inc(s_job, 1)

            for n in range(KT):
                c = n // 4
                for kind, first in (("cc", 2), ("cx", 4), ("cb", 0)):
                    feat_job(kind, n, chunk(("in", first + c)), hT)
            for j in range(2 * NT):
                i, half = divmod(j, 2)
                ps = open_job("oT", j)
                pe.wait_ge(s_on, i + 1)
                for h in range(4):
                    hd = 4 * half + h
                    last = tr(ps[:, P * h:P * (h + 1)], o_tok[:, i, P * hd:P * (hd + 1)], ident[:, :])
                last.then_inc(s_job, 1)
            emptied(pe, INDEX[("cb", KT - 1)])
            emptied(pe, INDEX[("oT", 2 * NT - 1)])
            for n in range(KT):
                c = n // 4
                for kind, name, src in (("gc", ("in", 12 + c), hT), ("cv", ("conv", c), uT), ("ga", ("in", 14 + c), hT), ("at", ("attn", c), oT)):
                    feat_job(kind, n, chunk(name), src)
            pe.wait_ge(s_mixT, KT)
            for j in range(2 * NT):
                n, i = divmod(j, NT)
                ps = open_job("wo", j)
                w = chunk(("o", n))
                for k in range(KT):
                    last = mm(ps[:, 0:512], mixT[:, k, P * i:P * (i + 1)], w[:, k, :], start=(k == 0), stop=(k == KT - 1))
                last.then_inc(s_job, 1)
            for i in range(NT):
                ps = open_job("h2T", i)
                pe.wait_ge(s_h2, i + 1)
                for k in range(KT):
                    last = tr(ps[:, P * k:P * (k + 1)], h2[:, i, P * k:P * (k + 1)], ident[:, :])
                last.then_inc(s_job, 1)
            ps = open_job("route", 0)
            pe.wait_ge(s_rwts, 16)
            rw = rwts[:, :].rearrange("p (k n) -> p k n", k=KT)
            for i in range(NT):
                emptied(pe, INDEX[("h2T", i)])
                for k in range(KT):
                    last = mm(ps[:, 20 * i:20 * (i + 1)], h2T[:, i, k, :], rw[:, k, :], start=(k == 0), stop=(k == KT - 1))
            last.then_inc(s_job, 1)
            ps = open_job("rank", 0)
            pe.wait_ge(s_mask, 1)
            both = rt[:, 660:740]
            for i in range(NT):
                for j in range(i + 1):
                    last = mm(ps[:, 16 * i:16 * (i + 1)], (tri if j == i else ones)[:, :], both[:, 16 * j:16 * (j + 1)], start=(j == 0), stop=(j == i))
            for j in range(NT):
                last = mm(ps[:, 80:96], ones[:, :], both[:, 16 * j:16 * (j + 1)], start=(j == 0), stop=(j == NT - 1))
            last.then_inc(s_job, 1)
            emptied(pe, INDEX[("rank", 0)])

            def tokens_T(k, gathered, value, b):
                pe.wait_ge(gathered, value)
                for t in range(KT):
                    last = tr(psum[:, P * t:P * (t + 1)], xg[b][:, P * t:P * (t + 1)], ident[:, :])
                last.then_inc(s_T, 1)

            def gate_up(k, loaded, value, b):
                pe.wait_ge(s_xgT, k + 1)
                pe.wait_ge(loaded, value)
                for j in range(2):
                    w = slot[2 * b + j].rearrange("p (k n) -> p k n", k=KT)
                    for t in range(KT):
                        last = mm(psum[:, 1024 + 512 * j:1536 + 512 * j], xgT[:, t, :], w[:, t, :], start=(t == 0), stop=(t == KT - 1))
                last.then_inc(s_gu, 1)

            def hidden_T(k):
                pe.wait_ge(s_hh, k + 1)
                for t in range(4):
                    last = tr(psum[:, 2048 + P * t:2048 + P * (t + 1)], hh[:, P * t:P * (t + 1)], ident[:, :])
                last.then_inc(s_HT, 1)

            def down_proj(k, loaded, value, b, first=False):
                pe.wait_ge(s_hhT, k + 1)
                if not first:
                    pe.wait_ge(s_ydve, k)
                    pe.wait_ge(s_yact, k)
                if loaded is not None:
                    pe.wait_ge(loaded, value)
                w = down[b].rearrange("p (k n) -> p k n", k=4)
                for half in range(2):
                    for t in range(4):
                        last = mm(psum[:, 2560 + 512 * half:3072 + 512 * half], hhT[:, t, :], w[:, t, 512 * half:512 * (half + 1)],
                                  start=(t == 0), stop=(t == 3))
                last.then_inc(s_d, 1)

            tokens_T(0, s_xg[0], 16, 0)
            gate_up(0, s_wgu[0], 32, 0)
            tokens_T(1, s_xg[1], 16, 1)
            hidden_T(0)
            gate_up(1, s_wgu[1], 32, 1)
            tokens_T(2, s_xg[2], 16, 2)
            down_proj(0, s_wd[0], 16, 0, first=True)
            hidden_T(1)
            gate_up(2, s_wgu[0], 64, 0)
            tokens_T(3, s_xg[3], 16, 3)
            down_proj(1, s_wd[1], 16, 1)
            hidden_T(2)
            with pe.Fori(0, 3) as it:
                for j in range(4):
                    e, b = 4 * it + 3 + j, (1 + j) % 2
                    gate_up(e, s_wgu[b], it * 64 + 32 * ((3 + j) // 2 + 1), b)
                    tokens_T(e + 1, s_xg[j], it * 16 + 32, j)
                    down_proj(e - 1, s_wd[1 - b], it * 32 + 16 * ((2 + j) // 2 + 1), 1 - b)
                    hidden_T(e)
            gate_up(15, s_wgu[1], 32 * 8, 1)
            down_proj(14, s_wd[0], 16 * 8, 0)
            hidden_T(15)
            down_proj(15, s_wd[1], 16 * 8, 1)

            def more(e, c, k):
                tokens_T(k + EXPERTS, s_ofx, (k + 1) * 16, 0)
                gate_up(k + EXPERTS, s_ofw, (k + 1) * 48, 0)
                hidden_T(k + EXPERTS)
                down_proj(k + EXPERTS, None, 0, 0)

            more_chunks(pe, more)


def rope_tables():
    grid_w, axis = 64, QK // 2
    tok = np.arange(N_LAT)
    pos = np.stack([tok // grid_w, tok % grid_w], axis=1).astype(np.float32)
    inv = (1.0 / (np.float32(10000.0) ** (np.arange(0, axis, 2, dtype=np.float32) / np.float32(axis)))).astype(np.float32)
    ang = pos[:, :, None, None] * inv[None, None, None, :]
    cos = np.broadcast_to(np.cos(ang), (N_LAT, 2, 2, 16)).reshape(4, P, 64)
    sin = (np.sin(ang) * np.array([-1.0, 1.0], np.float32)[None, None, :, None]).reshape(4, P, 64)
    return np.ascontiguousarray(np.stack([cos, sin]).transpose(2, 0, 1, 3).reshape(P, 512).astype(np.float32))


def kernel(**inputs):
    import concourse.bacc as bacc
    from concourse.bass_utils import run_bass_kernel_spmd

    x = {name: np.asarray(value) for name, value in inputs.items()}
    flat = {name: x[name][0] for name in ("w_ada", "w_in", "w_conv_out", "w_attn_out", "w_o", "w1", "w3", "w2")}

    def by_partition(a):
        return a.reshape(-1, P).T

    cT = np.stack([by_partition(x["c"][0]), by_partition(x["c_ctx"])], axis=2).reshape(P, 16)
    tokid = (np.arange(NT)[None, :] * P + np.arange(P)[:, None]).astype(np.float32)
    conv = x["conv_w"][0].reshape(3, KT, P).transpose(2, 0, 1).reshape(P, 24)
    cols = np.concatenate([by_partition(x["b_ada"][0]), by_partition(x["norm1_g"][0]), by_partition(x["norm2_g"][0]), conv,
                           x["subln_g"][0].reshape(P, 1), cT, tokid], axis=1)
    rows = np.concatenate([x["q_norm_g"][0], x["k_norm_g"][0], x["lambda_q1"][0], x["lambda_k1"][0], x["lambda_q2"][0], x["lambda_k2"][0],
                           x["b_grp"][0], x["b_exp"][0], np.array([4, 3, 2, 1], np.float32), np.arange(EXPERTS, dtype=np.float32) * CHUNKS])
    w_route = np.concatenate([x["w_grp"][0], x["w_exp"][0]], axis=1).reshape(KT, P, 20).transpose(1, 0, 2).reshape(P, KT * 20)
    arrays = {
        "x_prompt": x["x_prompt"][0], "x_sample": x["x_sample"][0], "cache_k": x["cache_k"].reshape(P, D), "cache_v": x["cache_v"].reshape(P, D),
        "cols": cols, "rows": rows.reshape(1, ROWS), "w_route": w_route, "rope": rope_tables(), **flat,
    }
    arrays = {name: np.ascontiguousarray(a) for name, a in arrays.items()}
    nc = bacc.Bacc("TRN2", target_bir_lowering=False, num_devices=1)
    f32, u32 = mybir.dt.float32, mybir.dt.uint32
    io = {name: nc.dram_tensor("in_" + name, a.shape, f32, kind="ExternalInput").ap() for name, a in arrays.items()}
    outs = {"y_prompt": (N_CTX, D), "y_sample": (N_LAT, D), "new_k": (P, D), "new_v": (P, D)}
    for name, shape in outs.items():
        io[name] = nc.dram_tensor(name, shape, f32, kind="ExternalOutput").ap()
    for name, shape, dt in (("rows_scratch", (64, P), f32), ("h2_scratch", (T, D), f32), ("y_scratch", (PAIRS_ALL, D), f32),
                            ("table_scratch", (SLOTS, EXPERTS * CHUNKS), u32)):
        io[name] = nc.dram_tensor(name, shape, dt, kind="Internal").ap()
    build(nc, io)
    r = run_bass_kernel_spmd(nc, [{"in_" + name: a for name, a in arrays.items()}], core_ids=[0]).results[0]
    return (r["y_prompt"].reshape(1, N_CTX, D), r["y_sample"].reshape(1, N_LAT, D),
            r["new_k"].reshape(1, 1, P, HEADS, 2, QK), r["new_v"].reshape(1, 1, P, HEADS, P))
```
